# Optimizing a Trainium2 kernel written in Bass

```python
import jax, jax.numpy as jnp
from jax import lax
import numpy as np

D_MODEL = 1024
BATCH = 1
SEQ = 256
DEPTH = 2

HEAD_DIM = 128
A_GROUPS = 4
A_GROUP_DIM = 128
A_WIDTH = A_GROUPS * A_GROUP_DIM
CHUNK = 128
NSA_HEADS = 8
NSA_KV_GROUPS = 2
NSA_WIDTH = NSA_HEADS * HEAD_DIM
NSA_KV_WIDTH = 3 * 2 * NSA_KV_GROUPS * HEAD_DIM
CMP_BLOCK = 32
CMP_STRIDE = 16
SLC_BLOCK = 64
N_SELECT = 16
WINDOW = 512
Q_BLOCK = 32
MEM_TOKENS = 256
MEM_HEADS = 4
MEM_WIDTH = MEM_HEADS * HEAD_DIM
ROPE_DIM = HEAD_DIM // 4
ROPE_THETA = 500000.0
EPS = 1e-6
NEG_INF = -1e30
FORCED_SCORE = 1e4
IN_SIZES = (A_WIDTH, A_WIDTH, A_WIDTH,
            NSA_WIDTH, NSA_WIDTH, NSA_HEADS * 3, NSA_KV_WIDTH,
            MEM_WIDTH, MEM_WIDTH,
            3 * D_MODEL)
D_IN = sum(IN_SIZES)

kernel_name = "hybrid_gmlp_nsa_memory_block"

def rmsnorm(x, gain):
    x32 = x.astype(jnp.float32)
    y = x32 * lax.rsqrt(jnp.mean(x32 * x32, axis=-1, keepdims=True) + EPS)
    return (y * gain.astype(jnp.float32)).astype(x.dtype)

def layernorm(x, gain, bias):
    x32 = x.astype(jnp.float32)
    xc = x32 - jnp.mean(x32, axis=-1, keepdims=True)
    y = xc * lax.rsqrt(jnp.mean(xc * xc, axis=-1, keepdims=True) + EPS)
    return (y * gain.astype(jnp.float32) + bias.astype(jnp.float32)).astype(x.dtype)

def rope_tables(positions):
    inv_freq = ROPE_THETA ** (-jnp.arange(0, ROPE_DIM, 2, dtype=jnp.float32) / ROPE_DIM)
    ang = positions.astype(jnp.float32)[..., None] * inv_freq
    return jnp.cos(ang)[:, :, None, :], jnp.sin(ang)[:, :, None, :]

def apply_partial_rope(t, cos, sin):
    half = ROPE_DIM // 2
    t1 = t[..., :half].astype(jnp.float32)
    t2 = t[..., half:ROPE_DIM].astype(jnp.float32)
    rot = jnp.concatenate([t1 * cos - t2 * sin, t2 * cos + t1 * sin], axis=-1).astype(t.dtype)
    return jnp.concatenate([rot, t[..., ROPE_DIM:]], axis=-1)

def chunk_spatial_gating(u, v, ln_g, ln_b, w_s, b_s):
    B, S, _ = v.shape
    vn = layernorm(v, ln_g, ln_b).reshape(B, S // CHUNK, CHUNK, A_GROUPS, A_GROUP_DIM)
    ws = w_s * jnp.tril(jnp.ones((CHUNK, CHUNK), w_s.dtype))
    mixed = jnp.einsum('gts,bnsgc->bntgc', ws, vn) + b_s.T[:, :, None]
    return u * mixed.reshape(B, S, A_WIDTH)

def compress_blocks(t, pe, w1, w2):
    B, S, G, Dh = t.shape
    tb = t.reshape(B, S // CMP_STRIDE, CMP_STRIDE, G, Dh)
    blocks = jnp.concatenate([tb[:, :-1], tb[:, 1:]], axis=2) + pe[:, None, :]
    h = jax.nn.silu(jnp.einsum('bnlgd,ldh->bngh', blocks, w1))
    return jnp.einsum('bngh,hd->bngd', h, w2)

def cmp_to_slc_matrix(n_cmp, n_slc):
    i = np.arange(n_cmp)[:, None] * CMP_STRIDE
    j = np.arange(n_slc)[None, :] * SLC_BLOCK
    ov = np.clip(np.minimum(i + CMP_BLOCK, j + SLC_BLOCK) - np.maximum(i, j), 0, None)
    return jnp.asarray(ov / CMP_BLOCK, dtype=jnp.float32)

def nsa_attention(q, k_cmp, v_cmp, k_slc, v_slc, k_win, v_win, gates):
    B, S, H, Dh = q.shape
    G = NSA_KV_GROUPS
    R = H // G
    n_cmp = k_cmp.shape[1]
    n_slc = S // SLC_BLOCK
    n_sel = min(N_SELECT, n_slc)
    nb = S // Q_BLOCK
    scale = Dh ** -0.5
    cmp_end = jnp.arange(n_cmp) * CMP_STRIDE + (CMP_BLOCK - 1)
    m_cs = cmp_to_slc_matrix(n_cmp, n_slc)
    ks_blk = k_slc.reshape(B, n_slc, SLC_BLOCK, G, Dh).transpose(0, 3, 1, 2, 4)
    vs_blk = v_slc.reshape(B, n_slc, SLC_BLOCK, G, Dh).transpose(0, 3, 1, 2, 4)
    kw_pad = jnp.pad(k_win, ((0, 0), (WINDOW, 0), (0, 0), (0, 0)))
    vw_pad = jnp.pad(v_win, ((0, 0), (WINDOW, 0), (0, 0), (0, 0)))
    b_ix = jnp.arange(B)[:, None, None, None]
    g_ix = jnp.arange(G)[None, None, :, None]
    slc_off = jnp.arange(SLC_BLOCK)
    blk_ids = jnp.arange(n_slc)

    def one_block(args):
        qb, gb, blk = args
        s0 = blk * Q_BLOCK
        t = s0 + jnp.arange(Q_BLOCK)
        sc = jnp.einsum('btgrd,bngd->bgrtn', qb, k_cmp).astype(jnp.float32) * scale
        cmask = cmp_end[None, :] <= t[:, None]
        pc = jax.nn.softmax(jnp.where(cmask, sc, NEG_INF), axis=-1) * cmask
        o_cmp = jnp.einsum('bgrtn,bngd->btgrd', pc.astype(qb.dtype), v_cmp)
        imp = jnp.einsum('bgrtn,nj->btgj', pc, m_cs)
        cur = (t // SLC_BLOCK)[None, :, None, None]
        forced = (blk_ids == 0) | (blk_ids == cur) | (blk_ids == cur - 1)
        imp = jnp.where(forced, FORCED_SCORE, jnp.where(blk_ids <= cur, imp, -1.0))
        _, idx = lax.top_k(imp, n_sel)
        kg = ks_blk[b_ix, g_ix, idx]
        vg = vs_blk[b_ix, g_ix, idx]
        ss = jnp.einsum('btgrd,btgkld->btgrkl', qb, kg).astype(jnp.float32) * scale
        tok = idx[..., None] * SLC_BLOCK + slc_off
        smask = (tok <= t[None, :, None, None, None])[:, :, :, None]
        ss = jnp.where(smask, ss, NEG_INF)
        ps = jax.nn.softmax(ss.reshape(B, Q_BLOCK, G, R, -1), axis=-1).reshape(ss.shape)
        o_slc = jnp.einsum('btgrkl,btgkld->btgrd', ps.astype(qb.dtype), vg)
        kw = lax.dynamic_slice_in_dim(kw_pad, s0, Q_BLOCK + WINDOW, axis=1)
        vw = lax.dynamic_slice_in_dim(vw_pad, s0, Q_BLOCK + WINDOW, axis=1)
        kpos = s0 - WINDOW + jnp.arange(Q_BLOCK + WINDOW)
        rel = t[:, None] - kpos[None, :]
        wmask = (rel >= 0) & (rel < WINDOW) & (kpos[None, :] >= 0)
        sw = jnp.einsum('btgrd,bsgd->bgrts', qb, kw).astype(jnp.float32) * scale
        pw = jax.nn.softmax(jnp.where(wmask, sw, NEG_INF), axis=-1)
        o_win = jnp.einsum('bgrts,bsgd->btgrd', pw.astype(qb.dtype), vw)
        gb = gb.reshape(B, Q_BLOCK, G, R, 3)
        return gb[..., 0:1] * o_cmp + gb[..., 1:2] * o_slc + gb[..., 2:3] * o_win

    q_blocks = q.reshape(B, nb, Q_BLOCK, G, R, Dh).transpose(1, 0, 2, 3, 4, 5)
    g_blocks = gates.reshape(B, nb, Q_BLOCK, H, 3).transpose(1, 0, 2, 3, 4)
    out = lax.map(one_block, (q_blocks, g_blocks, jnp.arange(nb)))
    return out.transpose(1, 0, 2, 3, 4, 5).reshape(B, S, H * Dh)

def memory_attention(q, k, v):
    B, S, H, Dh = q.shape
    s = jnp.einsum('bshd,bmhd->bhsm', q, k).astype(jnp.float32) * (Dh ** -0.5)
    p = jax.nn.softmax(s, axis=-1)
    return jnp.einsum('bhsm,bmhd->bshd', p.astype(q.dtype), v).reshape(B, S, H * Dh)

def setup_inputs(seed: int = 0) -> dict:
    key = jax.random.key(seed)
    ks = jax.random.split(key, 24)
    f32 = jnp.float32

    def nrm(k, shape, scale):
        return jax.random.normal(k, shape, f32) * scale

    x = nrm(ks[0], (BATCH, SEQ, D_MODEL), 1.0)
    mem = nrm(ks[1], (BATCH, MEM_TOKENS, D_MODEL), 1.0)
    offsets = jax.random.randint(ks[2], (BATCH, 1), 0, 4096, dtype=jnp.int32)
    positions = offsets + jnp.arange(SEQ, dtype=jnp.int32)[None, :]
    return {
        "x": x,
        "mem": mem,
        "positions": positions,
        "norm_gain": 1.0 + nrm(ks[3], (DEPTH, D_MODEL), 0.05),
        "w_in": nrm(ks[4], (DEPTH, D_MODEL, D_IN), D_MODEL ** -0.5),
        "ln_v_gain": 1.0 + nrm(ks[5], (DEPTH, A_WIDTH), 0.05),
        "ln_v_bias": nrm(ks[6], (DEPTH, A_WIDTH), 0.02),
        "w_spatial": nrm(ks[7], (DEPTH, A_GROUPS, CHUNK, CHUNK), 0.5 * CHUNK ** -0.5),
        "b_spatial": 1.0 + nrm(ks[8], (DEPTH, A_GROUPS, CHUNK), 0.1),
        "cmp_pe_k": nrm(ks[9], (DEPTH, CMP_BLOCK, HEAD_DIM), 0.1),
        "cmp_w1_k": nrm(ks[10], (DEPTH, CMP_BLOCK, HEAD_DIM, HEAD_DIM), (CMP_BLOCK * HEAD_DIM) ** -0.5),
        "cmp_w2_k": nrm(ks[11], (DEPTH, HEAD_DIM, HEAD_DIM), HEAD_DIM ** -0.5),
        "cmp_pe_v": nrm(ks[12], (DEPTH, CMP_BLOCK, HEAD_DIM), 0.1),
        "cmp_w1_v": nrm(ks[13], (DEPTH, CMP_BLOCK, HEAD_DIM, HEAD_DIM), (CMP_BLOCK * HEAD_DIM) ** -0.5),
        "cmp_w2_v": nrm(ks[14], (DEPTH, HEAD_DIM, HEAD_DIM), HEAD_DIM ** -0.5),
        "mem_norm_gain": 1.0 + nrm(ks[15], (D_MODEL,), 0.05),
        "w_mem_kv": nrm(ks[16], (DEPTH, D_MODEL, 2 * MEM_WIDTH), D_MODEL ** -0.5),
        "w_branch_a": nrm(ks[17], (DEPTH, A_WIDTH, D_MODEL), A_WIDTH ** -0.5),
        "w_branch_b": nrm(ks[18], (DEPTH, NSA_WIDTH, D_MODEL), NSA_WIDTH ** -0.5),
        "w_branch_c": nrm(ks[19], (DEPTH, MEM_WIDTH, D_MODEL), MEM_WIDTH ** -0.5),
        "w_out": nrm(ks[20], (DEPTH, D_MODEL, D_MODEL), D_MODEL ** -0.5),
        "final_norm_gain": 1.0 + nrm(ks[21], (D_MODEL,), 0.05),
    }

def reference(x, mem, positions, norm_gain, w_in, ln_v_gain, ln_v_bias, w_spatial, b_spatial,
              cmp_pe_k, cmp_w1_k, cmp_w2_k, cmp_pe_v, cmp_w1_v, cmp_w2_v, mem_norm_gain, w_mem_kv,
              w_branch_a, w_branch_b, w_branch_c, w_out, final_norm_gain):
    B, S, D = x.shape
    G = NSA_KV_GROUPS
    splits = [int(s) for s in np.cumsum(IN_SIZES)[:-1]]
    cos, sin = rope_tables(positions)
    mem_n = rmsnorm(mem, mem_norm_gain)
    for l in range(DEPTH):
        h = rmsnorm(x, norm_gain[l])
        proj = h @ w_in[l]
        a_u, a_v, a_z, b_q, b_z, b_g, b_kv, c_q, c_z, merge = jnp.split(proj, splits, axis=-1)
        o_a = chunk_spatial_gating(a_u, a_v, ln_v_gain[l], ln_v_bias[l], w_spatial[l], b_spatial[l])
        o_a = o_a * jax.nn.silu(a_z)
        q = apply_partial_rope(b_q.reshape(B, S, NSA_HEADS, HEAD_DIM), cos, sin)
        kv = b_kv.reshape(B, S, 3, 2, G, HEAD_DIM)
        k_cmp = compress_blocks(apply_partial_rope(kv[:, :, 0, 0], cos, sin), cmp_pe_k[l], cmp_w1_k[l], cmp_w2_k[l])
        v_cmp = compress_blocks(kv[:, :, 0, 1], cmp_pe_v[l], cmp_w1_v[l], cmp_w2_v[l])
        k_slc = apply_partial_rope(kv[:, :, 1, 0], cos, sin)
        k_win = apply_partial_rope(kv[:, :, 2, 0], cos, sin)
        gates = jax.nn.sigmoid(b_g).reshape(B, S, NSA_HEADS, 3)
        o_b = nsa_attention(q, k_cmp, v_cmp, k_slc, kv[:, :, 1, 1], k_win, kv[:, :, 2, 1], gates)
        o_b = o_b * jax.nn.silu(b_z)
        mkv = (mem_n @ w_mem_kv[l]).reshape(B, MEM_TOKENS, 2, MEM_HEADS, HEAD_DIM)
        o_c = memory_attention(c_q.reshape(B, S, MEM_HEADS, HEAD_DIM), mkv[:, :, 0], mkv[:, :, 1])
        o_c = o_c * jax.nn.silu(c_z)
        g = jax.nn.sigmoid(merge).reshape(B, S, 3, D)
        mixed = (g[:, :, 0] * (o_a @ w_branch_a[l]) + g[:, :, 1] * (o_b @ w_branch_b[l])
                 + g[:, :, 2] * (o_c @ w_branch_c[l]))
        x = x + mixed @ w_out[l]
    return rmsnorm(x, final_norm_gain)


_drawn_inputs = setup_inputs


def setup_inputs(seed=0):
    import zlib

    import numpy as np

    out = dict(_drawn_inputs(seed))
    spreads = {}
    factors = {'ln_v_gain': 7.064,
     'ln_v_bias': 28.478,
     'cmp_pe_k': 56.375,
     'cmp_pe_v': 4.681,
     'mem_norm_gain': 8.0,
     'cmp_w1_k': 2.865,
     'cmp_w2_k': 2.817}
    for name, (base, spread) in spreads.items():
        noise = np.random.default_rng([zlib.crc32(name.encode()), seed]).standard_normal(out[name].shape)
        drawn = base * np.exp(spread * noise) if base else spread * noise
        out[name] = __import__('jax').numpy.asarray(drawn.astype(out[name].dtype))
    for name, factor in factors.items():
        out[name] = (out[name] * factor).astype(out[name].dtype)
    return out
```

```python
from contextlib import ExitStack

import numpy as np

import concourse.bass as bass
from concourse import mybir

F32 = mybir.dt.float32
F32R = mybir.dt.float32r
I32 = mybir.dt.int32
ACT = mybir.ActivationFunctionType
ALU = mybir.AluOpType
AX = mybir.AxisListType

P = 128
D = 1024
S = 256
M = 256
DEPTH = 2
KT = D // P
HD = 128
HEADS = 8
GROUPS = 2
REP = HEADS // GROUPS
MH = 4
AW = 512
AG = 4
CB, CS = 32, 16
NCMP = 16
HALF = 16
ROT = 32
EPS = 1e-6
NEG = -1e30
SCALE = float(HD) ** -0.5
THETA = 500000.0
TWO_PI_HI = 6.28125
TWO_PI_MID = 0.0019350051879882812
TWO_PI_LO = 3.0199159819585e-07
INV_TWO_PI = 0.15915494309189535
ROUND = 12582912.0
PI_IN = 3.1415925
CW = 1024
RAW = 4
SPL = 4
HEAD = 12
LEAD = 3

BLOCKS = (["MK0", "MK1", "MV0", "MV1", "KC", "VC", "KS", "KW", "VS", "VW", "AV0", "AV1", "AU0", "AU1", "AZ0", "AZ1",
           "WK0", "WK1", "WV0", "WV1", "Q0", "Q1", "Q2", "Q3", "CQ0", "CQ1", "CZ0", "CZ1", "BZ0", "BZ1", "BZ2", "BZ3"]
          + [f"MG{i}" for i in range(12)] + [f"BR{i}" for i in range(8)] + [f"OUT{i}" for i in range(4)])
AT = {name: i for i, name in enumerate(BLOCKS)}
NB = len(BLOCKS)
NC = 2 * NB
KIND = ["".join(c for c in name if c.isalpha()) for name in BLOCKS]
TOKEN_MAJOR = ("MV", "VS", "VW", "AV", "OUT")
COPIED = ("MK", "MV", "KC", "VC", "KS", "KW", "VS", "VW", "AV", "AU", "Q", "CQ")
ROPED = ("KC", "KS", "KW", "Q")
GATED = ("AZ", "CZ", "BZ")
UNITS = ([("mem", h) for h in range(MH)]
         + [u for g in range(GROUPS) for u in ([("late", REP * g + i) for i in range(REP)]
                                              + [("early", REP * g), ("early", REP * g + 2)])])
NU = len(UNITS)
FIRST_SLOT = AT["CZ0"]
PV_OF = {}
for _u, (_k, _h) in enumerate(UNITS):
    if _k == "mem" or (_k == "late" and _h % REP == REP - 1) or (_k == "early" and _h % REP == 2):
        PV_OF[_u] = len(PV_OF)
NPV = len(PV_OF)


def halves(b):
    if b in (AT["OUT0"], AT["OUT1"]):
        return [(AT["OUT0"], b - AT["OUT0"]), (AT["OUT1"], b - AT["OUT0"])]
    return [(b, 0), (b, 1)]


def count_before(kinds, b):
    return sum(k in kinds for k in KIND[:b])


BLK_HI = {AT["VS"]: 0, AT["AU0"]: 1}
CMP_DIAG = {AT["WV0"]: 0, AT["Q0"]: 1}
CMP_TANH = {AT["WV0"]: 0, AT["Q0"]: 1}
CMP_OUT = {AT["Q0"]: 0, AT["Q2"]: 1}
OA_HI = {AT["WV0"]: 0, AT["WV1"]: 1}

N_COPY, N_ROPE, N_GATED = (count_before(k, NB) for k in (COPIED, ROPED, GATED))
PAR = {}
_at = 0
for _n, _w in (("gain", KT), ("pe_k", CB), ("pe_v", CB), ("wg", KT * 24), ("w2_k", HD), ("w2_v", HD), ("ws", AG * P)):
    PAR[_n] = slice(_at, _at + _w)
    _at += _w
NPAR = _at


def trunk(nc, x, mem, positions, stream, par, rows, mem_gain, final_gain, rot_consts, out):
    ctx = ExitStack()
    with ctx:
        def sb(name, shape, dt=F32):
            return ctx.enter_context(nc.sbuf_tensor(name, shape, dt))

        def sem(name):
            return ctx.enter_context(nc.semaphore(name))

        def bank(name, width=512):
            return ctx.enter_context(nc.psum_tensor(name, [P, width], F32))

        memory_hi = nc.dram_tensor("memory_hi", [P, KT * M], F32, kind="Internal").ap()
        memory_lo = nc.dram_tensor("memory_lo", [P, KT * M], F32, kind="Internal").ap()

        raw = sb("raw", [P, RAW, CW])
        w_hi = sb("w_hi", [P, SPL, CW], F32R)
        w_lo = sb("w_lo", [P, SPL, CW], F32R)
        xs = sb("xs", [P, 2, D])
        h_hi = sb("h_hi", [P, KT, S], F32R)
        h_lo = sb("h_lo", [P, KT, S], F32R)
        o_hi = sb("o_hi", [P, 16, S], F32R)
        o_lo = sb("o_lo", [P, 16, S], F32R)
        gates = sb("gates", [P, 24, S])
        xn = gates[:, 0:8, :].rearrange("p a b -> p (a b)").rearrange("p (t d) -> p t d", t=2)
        mems = gates[:, 8:16, :].rearrange("p a b -> p (a b)").rearrange("p (t d) -> p t d", t=2)
        kc = gates[:, 8:10, :]
        vc = gates[:, 10:12, :]
        blk = gates[:, 12:16, :].rearrange("p a b -> p (a b)").rearrange("p (l g n) -> p l g n", g=GROUPS, n=NCMP)
        vn = gates[:, 16:20, :].rearrange("p a b -> p (a b)").rearrange("p (t d) -> p t d", t=2)
        ua = gates[:, 20:24, :]
        zb = sb("zb", [P, HEADS, S])
        zc = sb("zc", [P, MH, S])
        q = sb("q", [P, HEADS, S])
        cq = sb("cq", [P, MH, S])
        mk = sb("mk", [P, MH, M])
        mv = sb("mv", [P, 2, AW])
        keys = sb("keys", [P, GROUPS, NCMP + 4 * P])
        vals = sb("vals", [P, 2, 2, GROUPS * HD])
        vcmp = sb("vcmp", [NCMP, GROUPS * HD])
        pt = sb("pt", [P, 4, 4 * P])
        ptc = sb("ptc", [NCMP, 4 * P])
        probs = sb("probs", [P, 2, NCMP + 2 * P])
        negmax = sb("negmax", [P, 2, 3])
        sums = sb("sums", [P, 2, 3])
        weight = sb("weight", [P, 2, 3])
        zt = sb("zt", [P, 512])
        ot = sb("ot", [P, 512])
        mix = sb("mix", [P, 3, S])
        rot = mix[0:ROT, 0:2, :].rearrange("p a n -> p (a n)")
        cosb = sb("cosb", [ROT, S])
        sinb = sb("sinb", [ROT, S])
        pos = zt[0:ROT, 0:S].bitcast(I32)
        rc = sb("rc", [ROT, 2])
        pars = sb("pars", [P, NPAR])
        lnb = sb("lnb", [P, 3, AW])
        mgain = sb("mgain", [P, KT])
        wg_hi = sb("wg_hi", [P, KT * 24], F32R)
        wg_lo = sb("wg_lo", [P, KT * 24], F32R)
        gt = mix[0:24, 2, :]
        bgate = sb("bgate", [P, 2, 24])
        ident = sb("ident", [P, P])
        identr = sb("identr", [P, P], F32R)
        fold = sb("fold", [P, 32])
        neg = sb("neg", [P, 2, NCMP + 2 * P], F32R)
        keep = sb("keep", [P, 2, NCMP])
        diag = sb("diag", [P, HD])
        hs = sb("hs", [P, 32])
        hst = sb("hst", [P, 32])
        sq = sb("sq", [P, 2, 4])
        ss = sb("ss", [P, 2])
        rstd = sb("rstd", [P, 2])
        minus_half = sb("minus_half", [P, 2])
        stats = sb("stats", [P, 2, 6])
        mvar = sb("mvar", [P, 2, 2])
        lstd = sb("lstd", [P, 2])

        pj = [bank("pj0"), bank("pj1")]
        sc = bank("sc", 1024)
        tr = bank("tr")
        tc = bank("tc")
        pv = bank("pv")
        mi = bank("mi")
        sc2 = sc[:, :].rearrange("p (j n) -> p j n", j=2)

        raw_in = [sem(f"raw_in{i}") for i in range(RAW)]
        mem_in = [sem("mem_in0"), sem("mem_in1")]
        x_in, consts_in, pars_in, memory_in = map(sem, ("x_in", "consts_in", "pars_in", "memory_in"))
        memory_out, out_done = sem("memory_out"), sem("out_done")
        hi_done, lo_done, chunk_used = sem("hi_done"), sem("lo_done"), sem("chunk_used")
        consts = sem("consts")
        wsm = sem("wsm")
        angle, trig, tables, const_step, mean_sq = map(sem, ("angle", "trig", "tables", "const_step", "mean_sq"))
        summed, squares, rstd_ready, xn_ready = sem("summed"), sem("squares"), sem("rstd_ready"), sem("xn_ready")
        h_tr, h_hi_done, h_lo_done = sem("h_tr"), sem("h_hi_done"), sem("h_lo_done")
        copied, shuffled, roped, rope_step = sem("copied"), sem("shuffled"), sem("roped"), sem("rope_step")
        tanh_z, gated = sem("tanh_z"), sem("gated")
        tanh_m = sem("tanh_m")
        wg_split_hi, wg_split_lo = sem("wg_split_hi"), sem("wg_split_lo")
        g_mm, g_tanh, g_half, g_tr, g_ready = map(sem, ("g_mm", "g_tanh", "g_half", "g_tr", "g_ready"))
        v_stats, lstd_step, vn_scaled, vn_gained, vn_ready = map(
            sem, ("v_stats", "lstd_step", "vn_scaled", "vn_gained", "vn_ready"))
        ua_ready, mixed_a, oa_sum, oa_prod, oa_hi, oa_lo = map(
            sem, ("ua_ready", "mixed_a", "oa_sum", "oa_prod", "oa_hi", "oa_lo"))
        blk_ready, blk_hi, blk_lo = sem("blk_ready"), sem("blk_hi"), sem("blk_lo")
        diag_ready, cmp_sum, cmp_tanh, cmp_act, cmp_mm, cmp_ready = map(
            sem, ("diag_ready", "cmp_sum", "cmp_tanh", "cmp_act", "cmp_mm", "cmp_ready"))
        scores, maxed, expd, wstep, weighted = sem("scores"), sem("maxed"), sem("expd"), sem("wstep"), sem("weighted")
        turned, pt_ready, pv_done, o_prod, ob_hi, ob_lo = map(
            sem, ("turned", "pt_ready", "pv_done", "o_prod", "ob_hi", "ob_lo"))
        mix_prod, mix_add, mix_hi, mix_lo = sem("mix_prod"), sem("mix_add"), sem("mix_hi"), sem("mix_lo")
        x_added, gained, fin = sem("x_added"), sem("gained"), [sem("fin0"), sem("fin1")]
        last_done, last_added = sem("last_done"), sem("last_added")

        def after(eng, s, n):
            if n > 0:
                eng.wait_ge(s, n)

        def wait_block(eng, l, b):
            eng.wait_ge(chunk_used, l * NC + (2 * b + 3 if b == AT["OUT0"] else 2 * b + 2))

        def n_copied(l, name):
            return l * N_COPY + count_before(COPIED, AT[name]) + 1

        def n_roped(l, name):
            return l * N_ROPE + count_before(ROPED, AT[name]) + 1

        def n_gated(l, name):
            return l * N_GATED + count_before(GATED, AT[name]) + 1

        def wait_evacuated(eng, l, b):
            p = b - 2
            while p >= 0 and KIND[p] in ("WK", "WV"):
                p -= 2
            if p < 0:
                l, p = l - 1, p + NB
            if l < 0:
                return
            k, name = KIND[p], BLOCKS[p]
            if k in COPIED:
                eng.wait_ge(copied, n_copied(l, name))
            elif k in GATED:
                eng.wait_ge(gated, n_gated(l, name))
            elif k == "MG":
                eng.wait_ge(tanh_m, 12 * l + p - AT["MG0"] + 1)
            elif k == "BR":
                eng.wait_ge(mix_prod, 8 * l + p - AT["BR0"] + 1)
            else:
                eng.wait_ge(x_added, 4 * l + p - AT["OUT0"] + 1)

        def key_view(part, branch):
            return keys[0:part, :, NCMP:].rearrange("p g (t b n) -> p g t b n", t=2, b=2)[:, :, :, branch, :]

        def oa_view(t):
            return ua[:, :, P * t:P * t + P]

        def probs_mem():
            return probs[:, :, :].rearrange("p a b -> p (a b)")[:, 0:512].rearrange("p (t n) -> p t n", t=2)

        def out_place(part, u):
            kind, h = UNITS[u]
            if kind == "mem":
                return part[:, 12 + h, :]
            g = h // REP
            t = 1 if kind == "late" else 0
            return part[:, 4 + REP * g:4 + REP * (g + 1), P * t:P * t + P]

        def out_source(u):
            return ot[:, 0:256] if UNITS[u][0] == "mem" else ot[:, :].rearrange("p (h n) -> p h n", h=REP)

        def copy_target(b):
            k, name = KIND[b], BLOCKS[b]
            i = int(name[len(k):] or 0)
            return {"MK": lambda: mk[:, 2 * i:2 * i + 2, :], "MV": lambda: mv[:, :, 256 * i:256 * i + 256],
                    "KC": lambda: kc, "VC": lambda: vc, "KS": lambda: key_view(P, 0), "KW": lambda: key_view(P, 1),
                    "VS": lambda: vals[:, :, 0, :], "VW": lambda: vals[:, :, 1, :],
                    "AV": lambda: vn[:, :, 256 * i:256 * i + 256], "AU": lambda: ua[:, 2 * i:2 * i + 2, :],
                    "Q": lambda: q[:, 2 * i:2 * i + 2, :], "CQ": lambda: cq[:, 2 * i:2 * i + 2, :]}[k]()

        def bank_view(b):
            v = pj[b % 2]
            if KIND[b] in ("KS", "KW"):
                return v[:, :].rearrange("p (g t n) -> p g t n", g=2, t=2)
            return v[:, :].rearrange("p (a n) -> p a n", a=2)

        def rope_view(b):
            k = KIND[b]
            if k in ("KS", "KW"):
                t = key_view(ROT, 0 if k == "KS" else 1)
                r = rot.rearrange("p (g t n) -> p g t n", g=2, t=2)
                tab = [y[:, :].rearrange("p (t n) -> p t n", t=2).unsqueeze(1).to_broadcast([ROT, 2, 2, P])
                       for y in (cosb, sinb)]
                return t, r, *tab
            t = copy_target(b)[0:ROT]
            r = rot.rearrange("p (a n) -> p a n", a=2)
            return t, r, *[y[:, :].unsqueeze(1).to_broadcast([ROT, 2, S]) for y in (cosb, sinb)]

        block = ctx.enter_context(nc.Block())

        @block.sync
        def _(sp):
            rounds = stream.rearrange("(r s) p w -> r s p w", s=RAW)

            sp.dma_start(mems[:, 0, :], mem[0:P, :]).then_inc(mem_in[0], 16)
            for l in range(DEPTH):
                if l:
                    wait_block(sp, l - 1, AT["BR7"])
                    sp.wait_ge(memory_out, 32)
                    sp.dma_start(o_hi[:, 0:KT, :].rearrange("p k m -> p (k m)").bitcast(F32), memory_hi).then_inc(memory_in, 16)
                    sp.dma_start(o_lo[:, 0:KT, :].rearrange("p k m -> p (k m)").bitcast(F32), memory_lo).then_inc(memory_in, 16)
                for i in range(HEAD):
                    if l == 0 and i == 4:
                        sp.dma_start(xs[:, :, :], x.rearrange("(t p) d -> p t d", p=P)).then_inc(x_in, 16)
                    if i == 6:
                        after(sp, cmp_ready, 2 * l)
                        after(sp, oa_sum, 2 * l)
                        after(sp, h_lo_done, KT * (l + 1) if l else 0)
                        sp.dma_start(pars[:, :], par[l]).then_inc(pars_in, 16)
                        sp.dma_start(lnb[:, :, :], rows[l:l + 1].to_broadcast([P, 3, AW])).then_inc(pars_in, 16)
                    if l or i >= RAW:
                        sp.wait_ge(lo_done, l * NC + i - RAW + 1)
                    sp.dma_start(raw[:, i % RAW, :], stream[l * NC + i]).then_inc(raw_in[i % RAW], 16)
                    if l == 0 and i == 9:
                        sp.wait_ge(h_lo_done, KT)
                        sp.wait_ge(h_hi_done, KT)
                        sp.dma_start(memory_hi, o_hi[:, 0:KT, :].rearrange("p k m -> p (k m)").bitcast(F32)).then_inc(memory_out, 16)
                        sp.dma_start(memory_lo, o_lo[:, 0:KT, :].rearrange("p k m -> p (k m)").bitcast(F32)).then_inc(memory_out, 16)
                with sp.Fori((l * NC + HEAD) // RAW, (l + 1) * NC // RAW) as ring:
                    for slot in range(RAW):
                        sp.wait_ge(lo_done, ring * RAW + (slot - RAW + 1))
                        sp.dma_start(raw[:, slot, :], rounds[ring, slot]).then_inc(raw_in[slot], 16)
            sp.wait_ge(oa_sum, 2 * DEPTH)
            sp.dma_start(lnb[:, 0:2, :].rearrange("p a n -> p (a n)"),
                         final_gain.to_broadcast([P, D])).then_inc(pars_in, 16)
            for t in range(2):
                sp.wait_ge(fin[t], 1)
                sp.dma_start(out[t * P:(t + 1) * P, :], xn[:, t, :]).then_inc(out_done, 16)
            sp.wait_ge(memory_out, 32)
            sp.wait_ge(out_done, 32)

        @block.tensor
        def _(pe):
            def three(dst, a_hi, a_lo, b_hi, b_lo, first, last):
                pe.matmul(dst, a_hi, b_hi, start=first, stop=False, skip_group_check=True)
                pe.matmul(dst, a_lo, b_hi, start=False, stop=False, skip_group_check=True)
                return pe.matmul(dst, a_hi, b_lo, start=False, stop=last, skip_group_check=True)

            def transposes_in(n, src):
                if n == 0:
                    pe.wait_ge(consts, 2)
                banks = [sc[:, 0:512], sc[:, 512:1024], tr, tc]
                for t in range(2):
                    pe.wait_ge(xn_ready, 2 * n + t + 1)
                    for j in range(4):
                        for k in range(2):
                            mm = pe.transpose(banks[j][:, 256 * k + P * t:256 * k + P * t + P],
                                              src[:, t, (2 * j + k) * P:(2 * j + k + 1) * P], ident[:, :])
                        if t:
                            mm.then_inc(h_tr, 1)

            def work(l, step, part):
                c = l * NC + 2 * step + part
                b, half = halves(step)[part]
                s = c % SPL
                k = KIND[b]
                pe.wait_ge(lo_done, c + 1)
                if half == 0 and k not in ("WK", "WV"):
                    wait_evacuated(pe, l, b)
                p = pj[b % 2]
                whi, wlo = w_hi[:, s, :], w_lo[:, s, :]
                if k in ("WK", "WV"):
                    acc = sc[:, 0:512] if k == "WK" else sc[:, 512:1024]
                    o0 = 0 if k == "WK" else 4
                    bh = o_hi[:, o0:o0 + 4, :].rearrange("p a b -> p (a b)")
                    bl = o_lo[:, o0:o0 + 4, :].rearrange("p a b -> p (a b)")
                    pair = 2 * (b - AT[k + "0"]) + half
                    for i in range(2):
                        l4 = 2 * pair + i
                        mm = three(acc, bh[:, P * l4:P * l4 + P], bl[:, P * l4:P * l4 + P],
                                   whi[:, 512 * i:512 * i + 512], wlo[:, 512 * i:512 * i + 512],
                                   l4 == 0, l4 == 7)
                elif k in TOKEN_MAJOR:
                    ah, al = (o_hi, o_lo) if k == "MV" else (h_hi, h_lo)
                    for t in range(2):
                        for j in range(4):
                            kt = 4 * half + j
                            mm = three(p[:, 256 * t:256 * t + 256], ah[:, kt, P * t:P * t + P],
                                       al[:, kt, P * t:P * t + P], whi[:, 256 * j:256 * j + 256],
                                       wlo[:, 256 * j:256 * j + 256],
                                       half == 0 and t == 0 and j == 0, half == 1 and j == 3)
                else:
                    for j in range(KT):
                        if k == "BR":
                            kt = KT * half + j
                            ah, al = o_hi, o_lo
                            if kt < 4:
                                dst, first, last = p[:, 0:256], kt == 0, kt == 3
                            elif kt < 12:
                                dst, first, last = p[:, 256:512], kt == 4, kt == 11
                            else:
                                dst, first, last = sc[:, 512 * (b % 2):512 * (b % 2) + 256], kt == 12, kt == 15
                        else:
                            kt = j
                            ah, al = (o_hi, o_lo) if k == "MK" else (h_hi, h_lo)
                            dst, first, last = p[:, 256 * half:256 * half + 256], j == 0, j == KT - 1
                            if half == 0 and (b == AT["KC"] or (l == 0 and b == 0)):
                                pe.wait_ge(h_lo_done, KT * (l + 1 if b else 0) + kt + 1)
                        wh, wl = whi[:, P * j:P * j + P], wlo[:, P * j:P * j + P]
                        mm = three(dst, wh, wl, ah[:, kt, :], al[:, kt, :], first, last)
                mm.then_inc(chunk_used, 1)

            def last_block():
                l, b = DEPTH - 1, AT["OUT3"]
                wait_evacuated(pe, l, b)
                for t in range(2):
                    if t:
                        pe.wait_ge(x_added, 4 * l + 3)
                    for half in range(2):
                        c = l * NC + 2 * b + half
                        pe.wait_ge(lo_done, c + 1)
                        whi, wlo = w_hi[:, c % SPL, :], w_lo[:, c % SPL, :]
                        for j in range(4):
                            kt = 4 * half + j
                            mm = three(pj[(b + t) % 2][:, 0:256], h_hi[:, kt, P * t:P * t + P],
                                       h_lo[:, kt, P * t:P * t + P], whi[:, 256 * j:256 * j + 256],
                                       wlo[:, 256 * j:256 * j + 256], kt == 0, kt == KT - 1)
                    mm.then_inc(last_done, 1)

            def branch_gates(l):
                pe.wait_ge(wg_split_lo, l + 1)
                for j in range(KT):
                    mm = three(tr[0:24, 0:S], wg_hi[:, 24 * j:24 * j + 24], wg_lo[:, 24 * j:24 * j + 24],
                               h_hi[:, j, :], h_lo[:, j, :], j == 0, j == KT - 1)
                mm.then_inc(g_mm, 1)

            def turn_gates(l):
                pe.wait_ge(g_half, l + 1)
                for t in range(2):
                    mm = pe.transpose(tc[:, 24 * t:24 * t + 24], gt[:, P * t:P * t + P], ident[0:24, 0:24])
                mm.then_inc(g_tr, 1)

            def spatial(l):
                pe.wait_ge(vn_ready, 2 * (l + 1))
                pe.wait_ge(wsm, l + 1)
                for t, dst in enumerate((mi, pv)):
                    for g in range(AG):
                        mm = pe.matmul(dst[:, P * g:P * g + P], vn[:, t, P * g:P * g + P],
                                       pars[:, PAR["ws"]][:, P * g:P * g + P], start=True, stop=True)
                    mm.then_inc(mixed_a, 1)

            def compress_sum(l, i):
                pe.wait_ge(diag_ready, 2 * l + i + 1)
                if l == 0 and i == 0:
                    pe.wait_ge(consts, 9)
                pe.wait_ge(g_ready, l + 1)
                after(pe, cmp_act, 2 * l + i)
                pe.matmul(tr[:, 0:32], diag[:, :], fold[:, :], start=True, stop=True).then_inc(cmp_sum, 1)

            def compress_out(l, i):
                pe.wait_ge(cmp_act, 2 * l + i + 1)
                if i == 0:
                    pe.matmul(tc[:, 0:32], pars[:, PAR["w2_k"]], hs[:, :], start=True, stop=True).then_inc(cmp_mm, 1)
                else:
                    pe.wait_ge(cmp_ready, 2 * l + 1)
                    for g in range(GROUPS):
                        mm = pe.matmul(tc[0:NCMP, HD * g:HD * g + HD], hs[:, NCMP * g:NCMP * g + NCMP],
                                       pars[:, PAR["w2_v"]], start=True, stop=True)
                    mm.then_inc(cmp_mm, 1)

            def score(l, u):
                kind, h = UNITS[u]
                if u == 0:
                    pe.wait_ge(diag_ready, 2 * l + 2)
                    pe.wait_ge(copied, n_copied(l, "CQ1"))
                after(pe, expd, l * NU + u)
                if l == 0 and u == 0:
                    pe.wait_ge(consts, 9)
                if kind == "mem":
                    for t in range(2):
                        mm = pe.matmul(sc[:, 256 * t:256 * t + 256], cq[:, h, P * t:P * t + P], mk[:, h, :],
                                       start=True, stop=True)
                    mm.then_inc(scores, 1)
                    return
                g = h // REP
                if u == MH:
                    pe.wait_ge(roped, n_roped(l, "Q3"))
                    pe.wait_ge(cmp_ready, 2 * l + 2)
                if kind == "late":
                    qq = q[:, h, P:2 * P]
                    pe.matmul(sc[:, 0:272], qq, keys[:, g, 0:272], start=True, stop=False)
                    pe.matmul(sc[:, 0:272], identr[:, :], neg[:, 1, :], start=False, stop=True)
                    pe.matmul(sc[:, 528:784], qq, keys[:, g, 272:528], start=True, stop=False)
                    pe.matmul(sc[:, 528:784], identr[:, :], neg[:, 0, NCMP:], start=False, stop=True).then_inc(scores, 1)
                else:
                    for j in range(2):
                        pe.matmul(sc[:, 512 * j:512 * j + 272], q[:, h + j, 0:P], keys[:, g, 0:272],
                                  start=True, stop=False)
                        mm = pe.matmul(sc[:, 512 * j:512 * j + 272], identr[:, :], neg[:, 0, :],
                                       start=False, stop=True)
                    mm.then_inc(scores, 1)

            def turn(l, u):
                kind, h = UNITS[u]
                pe.wait_ge(weighted, l * NU + u + 1)
                after(pe, pt_ready, l * NU + u)
                if kind == "mem":
                    pm = probs_mem()
                    for kt in range(2):
                        for t in range(2):
                            mm = pe.transpose(tr[:, 256 * kt + P * t:256 * kt + P * t + P],
                                              pm[:, t, P * kt:P * kt + P], ident[:, :])
                    mm.then_inc(turned, 1)
                    return
                for j in range(2):
                    for br in range(2):
                        pe.transpose(tr[:, 256 * br + P * j:256 * br + P * j + P],
                                     probs[:, j, NCMP + P * br:NCMP + P * br + P], ident[:, :])
                n = 1 if kind == "late" else 2
                for j in range(n):
                    at = P * (h % REP + j)
                    mm = pe.transpose(tc[0:NCMP, at:at + P], probs[:, j, 0:NCMP], ident[:, :])
                mm.then_inc(turned, 1)

            def values(l, u):
                kind, h = UNITS[u]
                i = PV_OF[u]
                pe.wait_ge(pt_ready, l * NU + u + 1)
                after(pe, o_prod, l * NPV + i)
                if i == 0:
                    pe.wait_ge(oa_sum, 2 * l + 2)
                if kind == "mem":
                    for kt in range(2):
                        mm = pe.matmul(pv[:, 0:256], mv[:, kt, P * h:P * h + P], pt[:, kt, 0:256],
                                       start=kt == 0, stop=kt == 1)
                    mm.then_inc(pv_done, 1)
                    return
                g = h // REP
                tiles = (0, 1) if kind == "late" else (0,)
                first = True
                for kt in tiles:
                    for br in range(2):
                        pe.matmul(pv[:, :], vals[:, kt, br, HD * g:HD * g + HD], pt[:, 2 * br + kt, :],
                                  start=first, stop=False)
                        first = False
                pe.matmul(pv[:, :], vcmp[:, HD * g:HD * g + HD], ptc[:, :], start=False, stop=True).then_inc(pv_done, 1)

            for l in range(DEPTH):
                if l == 0:
                    transposes_in(0, mems)
                else:
                    pe.wait_ge(memory_in, 32 * l)
                for b in range(NB):
                    if b == AT["MV1"]:
                        transposes_in(1 + l, xn)
                    if b == AT["WK0"]:
                        pe.wait_ge(blk_lo, 2 * l + 1)
                    if b == AT["WV0"]:
                        pe.wait_ge(blk_lo, 2 * l + 2)
                    if b == AT["BR0"]:
                        pe.wait_ge(oa_lo, 2 * (l + 1))
                        pe.wait_ge(oa_hi, 2 * (l + 1))
                        pe.wait_ge(ob_lo, NPV * (l + 1) - 1)
                        pe.wait_ge(ob_hi, NPV * (l + 1) - 1)
                    s = b - FIRST_SLOT
                    if KIND[b] == "BR":
                        if b - AT["BR0"] >= 2:
                            pe.wait_ge(mix_prod, 8 * l + b - AT["BR0"] - 1)
                        else:
                            pe.wait_ge(expd, NU * (l + 1))
                    if b == AT["OUT0"]:
                        pe.wait_ge(mix_lo, 8 * l + 4)
                    if b == AT["OUT1"]:
                        pe.wait_ge(mix_lo, 8 * (l + 1))
                    if l == DEPTH - 1 and b == AT["OUT3"]:
                        last_block()
                        continue
                    work(l, b, 0)
                    if b == AT["WK0"]:
                        spatial(l)
                    if b == AT["WV0"]:
                        compress_sum(l, 0)
                    if b == AT["Q0"]:
                        compress_sum(l, 1)
                    if 0 <= s < NU:
                        score(l, s)
                    if s >= 2 and s - 2 in PV_OF:
                        values(l, s - 2)
                    if 1 <= s <= NU:
                        turn(l, s - 1)
                    if b == AT["BR0"]:
                        pe.wait_ge(ob_lo, NPV * (l + 1))
                        pe.wait_ge(ob_hi, NPV * (l + 1))
                    work(l, b, 1)
                    if b == AT["WV1"]:
                        compress_out(l, 0)
                    if b == AT["Q1"]:
                        compress_out(l, 1)
                    if b == AT["AV0"]:
                        branch_gates(l)
                    if b == AT["AU0"]:
                        turn_gates(l)

        @block.scalar
        def _(act):
            def split(c):
                if c >= DEPTH * NC:
                    return
                act.wait_ge(raw_in[c % RAW], 16 * (c // RAW + 1))
                if c >= SPL:
                    act.wait_ge(chunk_used, c - SPL + 1)
                act.activation(w_hi[:, c % SPL, :], raw[:, c % RAW, :], ACT.Copy).then_inc(hi_done, 1)

            def square(n, src):
                if n == 1:
                    act.wait_ge(x_in, 16)
                    act.wait_ge(xn_ready, 2)
                for t in range(2):
                    if n == 0:
                        act.wait_ge(mem_in[t], 16)
                    act.activation(xn[:, t, :], src[:, t, :], ACT.Square,
                                   accum_out=sq[:, t, 0:1]).then_inc(squares, 1)

            def square_part(l, i):
                act.wait_ge(x_added, 4 * l + i + 1)
                a = 256 * i
                for t in range(2):
                    ins = act.activation(mems[:, t, a:a + 256], xs[:, t, a:a + 256], ACT.Square,
                                         accum_out=sq[:, t, i:i + 1])
                ins.then_inc(squares, 1)

            def norm_hi(n, hi, gain):
                banks = [sc[:, 0:512], sc[:, 512:1024], tr, tc]
                if n >= 2:
                    wait_block(act, n - 2, AT["OUT3"])
                for k in range(KT):
                    act.wait_ge(h_tr, 4 * n + k // 2 + 1)
                    act.activation(hi[:, k, :], banks[k // 2][:, 256 * (k % 2):256 * (k % 2) + 256], ACT.Copy,
                                   scale=gain[:, k:k + 1]).then_inc(h_hi_done, 1)

            def first_half(l, b):
                k = KIND[b]
                if k in COPIED:
                    wait_block(act, l, b)
                    if k == "MK" or k == "MV":
                        after(act, pv_done, NPV * l)
                    scale = SCALE if k in ("Q", "CQ") else 1.0
                    act.activation(copy_target(b), bank_view(b), ACT.Copy, scale=scale)\
                       .then_inc(copied, 1)
                elif k in GATED:
                    wait_block(act, l, b)
                    after(act, gated, l * N_GATED + count_before(GATED, b))
                    act.activation(zt[:, :], pj[b % 2][:, :], ACT.Tanh, scale=0.5).then_inc(tanh_z, 1)
                elif k == "MG":
                    i = b - AT["MG0"]
                    wait_block(act, l, b)
                    act.wait_ge(oa_lo, 2 * l + 2)
                    act.activation(gates[:, 2 * i:2 * i + 2, :], bank_view(b), ACT.Tanh, scale=0.5)\
                       .then_inc(tanh_m, 1)

            def exps(l, u):
                kind, h = UNITS[u]
                act.wait_ge(maxed, 2 * (l * NU + u + 1))
                after(act, turned, l * NU + u)
                if kind == "mem":
                    pm = probs_mem()
                    for t in range(2):
                        ins = act.activation(pm[:, t, :], sc[:, 256 * t:256 * t + 256], ACT.Exp,
                                             bias=negmax[:, 0, t:t + 1], accum_out=sums[:, 0, t:t + 1])
                elif kind == "late":
                    act.activation(probs[:, 0, 0:NCMP], sc[:, 0:NCMP], ACT.Exp, bias=negmax[:, 0, 0:1],
                                   accum_out=sums[:, 0, 0:1])
                    for br in range(2):
                        a = NCMP + P * br
                        ins = act.activation(probs[:, :, a:a + P], sc2[:, :, a:a + P], ACT.Exp,
                                             bias=negmax[:, 0, br + 1:br + 2], accum_out=sums[:, 0, br + 1:br + 2])
                else:
                    for j in range(2):
                        for i, (a, e) in enumerate(((0, NCMP), (NCMP, NCMP + P), (NCMP + P, NCMP + 2 * P))):
                            ins = act.activation(probs[:, j, a:e], sc[:, 512 * j + a:512 * j + e], ACT.Exp,
                                                 bias=negmax[:, j, i:i + 1], accum_out=sums[:, j, i:i + 1])
                ins.then_inc(expd, 1)

            def copy_turned(l, u):
                kind, h = UNITS[u]
                act.wait_ge(turned, l * NU + u + 1)
                n_before = sum(1 for v in PV_OF if v < u)
                after(act, pv_done, l * NPV + n_before)
                if kind == "mem":
                    act.activation(pt[:, 0:2, 0:256], tr[:, :].rearrange("p (k n) -> p k n", k=2),
                                   ACT.Copy).then_inc(pt_ready, 1)
                    return
                hh = h % REP
                trv = tr[:, :].rearrange("p (b j n) -> p b j n", b=2, j=2)
                if kind == "late":
                    dst = pt[:, :, P * hh:P * hh + P].rearrange("p (b j) n -> p b j n", b=2)
                    n = 1
                else:
                    dst = pt[:, :, P * hh:P * hh + 2 * P].rearrange("p (b k) (j n) -> p b k j n", b=2, j=2)[:, :, 0]
                    n = 2
                act.activation(dst, trv, ACT.Copy)
                act.activation(ptc[:, P * hh:P * (hh + n)], tc[0:NCMP, P * hh:P * (hh + n)],
                               ACT.Copy).then_inc(pt_ready, 1)

            def out_hi(l, u):
                i = PV_OF[u]
                act.wait_ge(o_prod, l * NPV + i + 1)
                act.activation(out_place(o_hi, u), out_source(u), ACT.Copy).then_inc(ob_hi, 1)

            def mix_high(l, i):
                act.wait_ge(mix_add, 2 * (8 * l + i + 1))
                act.activation(h_hi[:, i, :], mix[:, 0, :], ACT.Copy).then_inc(mix_hi, 1)

            act.dma_start(mems[:, 1, :], mem[P:2 * P, :]).then_inc(mem_in[1], 16)
            act.dma_start(mgain[:, :], mem_gain).then_inc(consts_in, 16)
            act.wait_ge(const_step, 5)
            act.activation(sums[:, 0, 0:2], minus_half[:, :], ACT.Square)
            act.dma_start(rc[:, :], rot_consts).then_inc(consts_in, 16)
            act.dma_start(pos, positions.to_broadcast([ROT, S])).then_inc(consts_in, 16)
            act.wait_ge(consts, 1)
            square(0, mems)
            split(0)
            split(1)
            act.wait_ge(consts_in, 48)
            norm_hi(0, o_hi, mgain)
            for c in range(2, LEAD):
                split(c)
            for l in range(DEPTH):
                for b in range(NB):
                    c = l * NC + 2 * b
                    s = b - FIRST_SLOT
                    if b in CMP_DIAG:
                        i = CMP_DIAG[b]
                        wait_block(act, l, b - 1)
                        after(act, cmp_sum, 2 * l + i)
                        for j in range(4):
                            ins = act.activation(diag[32 * j:32 * j + 32, :],
                                                 sc[32 * j:32 * j + 32, 512 * i + P * j:512 * i + P * j + P], ACT.Copy)
                        ins.then_inc(diag_ready, 1)
                    split(c + LEAD)
                    if 2 <= s < NU + 2:
                        copy_turned(l, s - 2)
                    if b > 0:
                        first_half(l, b - 1)
                    if b == AT["MV1"]:
                        norm_hi(1 + l, h_hi, pars[:, PAR["gain"]])
                    if b == AT["MV0"]:
                        act.wait_ge(pars_in, 32 * (l + 1))
                        after(act, g_mm, l)
                        act.activation(wg_hi[:, :], pars[:, PAR["wg"]], ACT.Copy).then_inc(wg_split_hi, 1)
                    if b == AT["AV1"]:
                        act.wait_ge(g_mm, l + 1)
                        act.activation(gt, tr[0:24, 0:S], ACT.Tanh, scale=0.5).then_inc(g_tanh, 1)
                    if b == AT["AU1"]:
                        act.wait_ge(g_tr, l + 1)
                        act.activation(bgate[:, :, :], tc[:, 0:48].rearrange("p (t n) -> p t n", t=2),
                                       ACT.Copy).then_inc(g_ready, 1)
                    if b in BLK_HI:
                        i = BLK_HI[b]
                        act.wait_ge(blk_ready, 6 * l + 3 * i + 3)
                        if l == 0 and i == 0:
                            act.wait_ge(memory_out, 32)
                        act.activation(o_hi[:, 4 * i:4 * i + 4, :].rearrange("p a b -> p (a b)"),
                                       blk.rearrange("p l g n -> p (l g n)"), ACT.Copy).then_inc(blk_hi, 1)
                    split(c + LEAD + 1)
                    if b in CMP_TANH:
                        i = CMP_TANH[b]
                        act.wait_ge(cmp_sum, 2 * l + i + 1)
                        act.activation(hst[:, :], tr[:, 0:32], ACT.Tanh, scale=0.5).then_inc(cmp_tanh, 1)
                    if b in CMP_OUT:
                        i = CMP_OUT[b]
                        act.wait_ge(cmp_mm, 2 * l + i + 1)
                        if i == 0:
                            act.activation(keys[:, :, 0:NCMP], tc[:, 0:32].rearrange("p (g n) -> p g n", g=2),
                                           ACT.Copy, scale=0.5).then_inc(cmp_ready, 1)
                        else:
                            act.activation(vcmp[:, :], tc[0:NCMP, 0:256], ACT.Copy, scale=0.5).then_inc(cmp_ready, 1)
                    if b in OA_HI:
                        t = OA_HI[b]
                        act.wait_ge(oa_prod, 2 * l + t + 1)
                        act.activation(o_hi[:, 0:4, P * t:P * t + P], oa_view(t), ACT.Copy).then_inc(oa_hi, 1)
                    if 0 <= s < NU:
                        exps(l, s)
                    if s - 2 in PV_OF:
                        out_hi(l, s - 2)
                    if 1 <= b - AT["BR0"] <= 8:
                        mix_high(l, b - AT["BR0"] - 1)
                    if l == 0 and b == AT["MK0"]:
                        square(1, xs)
                    if l == 0 and b == AT["MV0"]:
                        act.wait_ge(angle, 10)
                        act.activation(rot[:, 0:S], sinb[:, :], ACT.Sin)
                        act.activation(rot[:, S:2 * S], cosb[:, :], ACT.Sin).then_inc(trig, 1)
                    if b == AT["OUT2"]:
                        square_part(l, 0)
                        square_part(l, 1)
                    if b == AT["OUT3"]:
                        square_part(l, 2)
                if l < DEPTH - 1:
                    square_part(l, 3)
            for t in range(2):
                act.wait_ge(last_added, t + 1)
                act.activation(mems[:, t, 3 * 256:], xs[:, t, 3 * 256:], ACT.Square,
                               accum_out=sq[:, t, 3:4]).then_inc(squares, 1)
                if t == 0:
                    act.wait_ge(gained, 4)
                    act.wait_ge(rstd_ready, 2 * (DEPTH + 1) + 1)
                    act.activation(xn[:, 0, :], xn[:, 0, :], ACT.Copy, scale=rstd[:, 0:1]).then_inc(fin[0], 1)

        @block.vector
        def _(dve):
            swap = [(i + HALF) % ROT for i in range(ROT)]

            def split(c):
                if c >= DEPTH * NC:
                    return
                dve.wait_ge(hi_done, c + 1)
                if c >= SPL:
                    dve.wait_ge(chunk_used, c - SPL + 1)
                dve.tensor_tensor(w_lo[:, c % SPL, :], raw[:, c % RAW, :], w_hi[:, c % SPL, :].bitcast(F32),
                                  ALU.subtract).then_inc(lo_done, 1)

            def normalise(n, src, dst):
                for t in range(2):
                    dve.wait_ge(rstd_ready, 2 * n + t + 1)
                    dve.tensor_scalar(dst[:, t, :], src[:, t, :], rstd[:, t:t + 1], None, ALU.mult)\
                       .then_inc(xn_ready, 1)

            def row_sums(n):
                if n == 0:
                    for t in range(2):
                        dve.wait_ge(squares, t + 1)
                        dve.tensor_reduce(ss[:, t:t + 1], sq[:, t, :], AX.X, ALU.add).then_inc(summed, 1)
                    return
                dve.wait_ge(squares, 4 * n)
                dve.wait_ge(rstd_ready, 2 * n)
                dve.tensor_reduce(ss[:, :], sq[:, :, :], AX.X, ALU.add).then_inc(summed, 2)

            def norm_lo(n, hi, lo, gain):
                banks = [sc[:, 0:512], sc[:, 512:1024], tr, tc]
                for k in range(KT):
                    dve.wait_ge(h_hi_done, KT * n + k - k % 2 + 2)
                    dve.scalar_tensor_tensor(lo[:, k, :], banks[k // 2][:, 256 * (k % 2):256 * (k % 2) + 256],
                                             gain[:, k:k + 1], hi[:, k, :].bitcast(F32), ALU.mult,
                                             ALU.subtract).then_inc(h_lo_done, 1)

            def shuffle(l, b):
                i = l * N_ROPE + count_before(ROPED, b)
                dve.wait_ge(copied, n_copied(l, BLOCKS[b]))
                after(dve, roped, i)
                if i == 0:
                    dve.wait_ge(tables, 2)
                t, r, _, _ = rope_view(b)
                dve.stream_shuffle(r, t, swap).then_inc(shuffled, 1)

            def gate(l, b):
                k = KIND[b]
                i = b - AT[k + "0"]
                dve.wait_ge(tanh_z, l * N_GATED + count_before(GATED, b) + 1)
                if k == "AZ":
                    dst = ot[:, :]
                    after(dve, ob_lo, NPV * l)
                    after(dve, ob_hi, NPV * l)
                    after(dve, ua_ready, 2 * l + i)
                else:
                    dst = {"CZ": zc, "BZ": zb}[k][:, 2 * i:2 * i + 2, :].rearrange("p a n -> p (a n)")
                dve.scalar_tensor_tensor(dst, zt[:, :], 1.0, pj[b % 2][:, :], ALU.add, ALU.mult).then_inc(gated, 1)
                if k == "AZ":
                    dve.wait_ge(gated, n_gated(l, BLOCKS[b]))
                    dve.wait_ge(copied, n_copied(l, f"AU{i}"))
                    u2 = ua[:, 2 * i:2 * i + 2, :].rearrange("p a n -> p (a n)")
                    dve.scalar_tensor_tensor(u2, ot[:, :], 0.25, u2, ALU.mult, ALU.mult).then_inc(ua_ready, 1)

            def layernorm(l):
                dve.wait_ge(copied, n_copied(l, "AV1"))
                for t in range(2):
                    dve.bn_stats(stats[:, t, :], vn[:, t, :]).then_inc(v_stats, 1)
                dve.wait_ge(v_stats, 4 * l + 2)
                for t in range(2):
                    dve.bn_aggr(mvar[:, t, :], stats[:, t, :]).then_inc(v_stats, 1)

            def layernorm_scale(l):
                dve.wait_ge(v_stats, 4 * l + 4)
                dve.wait_ge(lstd_step, 2 * l + 2)
                for t in range(2):
                    dve.tensor_scalar(vn[:, t, :], vn[:, t, :], mvar[:, t, 0:1], lstd[:, t:t + 1], ALU.subtract,
                                      ALU.mult).then_inc(vn_scaled, 1)

            def mix_products(l, i):
                b = AT["BR0"] + i
                wait_block(dve, l, b)
                dve.wait_ge(tanh_m, 12 * (l + 1))
                after(dve, mix_lo, 8 * l + i)
                after(dve, mix_hi, 8 * l + i)
                for br in range(2):
                    dve.scalar_tensor_tensor(mix[:, br, :], gates[:, KT * br + i, :], 1.0,
                                             pj[b % 2][:, 256 * br:256 * br + 256], ALU.add, ALU.mult)
                a = 512 * (b % 2)
                dve.scalar_tensor_tensor(mix[:, 2, :], gates[:, 2 * KT + i, :], 1.0, sc[:, a:a + 256],
                                         ALU.add, ALU.mult).then_inc(mix_prod, 1)

            def add_out(l, i):
                b = AT["OUT0"] + i
                wait_block(dve, l, b)
                xv = xs[:, :, 256 * i:256 * i + 256]
                dve.tensor_tensor(xv, pj[b % 2][:, :].rearrange("p (t n) -> p t n", t=2), xv, ALU.add)\
                   .then_inc(x_added, 1)

            def maxima(l, u):
                kind, h = UNITS[u]
                dve.wait_ge(scores, l * NU + u + 1)
                after(dve, expd, l * NU + u)
                if kind == "mem":
                    for t in range(2):
                        dve.tensor_reduce(negmax[:, 0, t:t + 1], sc[:, 256 * t:256 * t + 256], AX.X, ALU.max,
                                          negate=True).then_inc(maxed, 1)
                elif kind == "late":
                    dve.tensor_reduce(negmax[:, 0, 0:1], sc[:, 0:NCMP], AX.X, ALU.max, negate=True).then_inc(maxed, 1)
                    dve.tensor_reduce(negmax[:, 0, 1:3],
                                      sc2[:, :, NCMP:NCMP + 2 * P].rearrange("p j (b n) -> p b j n", b=2),
                                      AX.XY, ALU.max, negate=True).then_inc(maxed, 1)
                else:
                    dve.tensor_reduce(negmax[:, :, 0:1], sc2[:, :, 0:NCMP], AX.X, ALU.max,
                                      negate=True).then_inc(maxed, 1)
                    dve.tensor_reduce(negmax[:, :, 1:3],
                                      sc2[:, :, NCMP:NCMP + 2 * P].rearrange("p j (b n) -> p j b n", b=2),
                                      AX.X, ALU.max, negate=True).then_inc(maxed, 1)

            def weigh(l, u):
                kind, h = UNITS[u]
                n = 2 * (l * NU + u)
                dve.wait_ge(expd, l * NU + u + 1)
                if kind == "mem":
                    dve.reciprocal(weight[:, 0, 0:2], sums[:, 0, 0:2]).then_inc(wstep, 2)
                    dve.wait_ge(wstep, n + 2)
                    pm = probs_mem()
                    for t in range(2):
                        ins = dve.tensor_scalar(pm[:, t, :], pm[:, t, :], weight[:, 0, t:t + 1], None, ALU.mult)
                    ins.then_inc(weighted, 1)
                    return
                late = kind == "late"
                m = 1 if late else 2
                tile = 1 if late else 0
                dve.reciprocal(weight[:, 0:m, :], sums[:, 0:m, :]).then_inc(wstep, 1)
                dve.wait_ge(wstep, n + 1)
                dve.tensor_tensor(weight[:, 0:m, :], weight[:, 0:m, :],
                                  bgate[:, tile, 3 * h:3 * h + 3 * m].rearrange("p (m n) -> p m n", m=m),
                                  ALU.mult).then_inc(wstep, 1)
                dve.wait_ge(wstep, n + 2)
                for j in range(m):
                    dve.scalar_tensor_tensor(probs[:, j, 0:NCMP], probs[:, j, 0:NCMP], weight[:, j, 0:1],
                                             keep[:, tile, :], ALU.mult, ALU.mult)
                    for br in range(2):
                        a = NCMP + P * br
                        v = probs[:, :, a:a + P] if late else probs[:, j, a:a + P]
                        ins = dve.tensor_scalar(v, v, weight[:, j, br + 1:br + 2], None, ALU.mult)
                ins.then_inc(weighted, 1)

            def out_product(l, u):
                kind, h = UNITS[u]
                i = PV_OF[u]
                dve.wait_ge(pv_done, l * NPV + i + 1)
                after(dve, ob_lo, l * NPV + i)
                after(dve, ob_hi, l * NPV + i)
                if kind == "mem":
                    dve.wait_ge(gated, n_gated(l, "CZ1"))
                    dve.scalar_tensor_tensor(ot[:, 0:256], pv[:, 0:256], 0.25, zc[:, h, :], ALU.mult, ALU.mult)\
                       .then_inc(o_prod, 1)
                    return
                dve.wait_ge(gated, n_gated(l, "BZ3"))
                g = h // REP
                t = 1 if kind == "late" else 0
                dve.scalar_tensor_tensor(ot[:, :].rearrange("p (h n) -> p h n", h=REP),
                                         pv[:, :].rearrange("p (h n) -> p h n", h=REP), 0.25,
                                         zb[:, REP * g:REP * g + REP, P * t:P * t + P], ALU.mult, ALU.mult)\
                   .then_inc(o_prod, 1)

            def reduce_angles():
                ang, turns = rot[:, 0:S], rot[:, S:2 * S]
                dve.wait_ge(consts_in, 48)
                dve.tensor_copy(cosb[:, :], pos).then_inc(angle, 1)
                dve.wait_ge(angle, 1)
                dve.tensor_scalar(ang, cosb[:, :], rc[:, 0:1], None, ALU.mult).then_inc(angle, 1)
                dve.wait_ge(angle, 2)
                dve.tensor_scalar(turns, ang, INV_TWO_PI, ROUND, ALU.mult, ALU.add).then_inc(angle, 1)
                dve.wait_ge(angle, 3)
                dve.tensor_scalar(turns, turns, ROUND, None, ALU.subtract).then_inc(angle, 1)
                for i, part in enumerate((TWO_PI_HI, TWO_PI_MID, TWO_PI_LO)):
                    dve.wait_ge(angle, 4 + i)
                    dve.scalar_tensor_tensor(ang, turns, -part, ang, ALU.mult, ALU.add).then_inc(angle, 1)
                dve.wait_ge(angle, 7)
                dve.tensor_scalar(sinb[:, :], ang, PI_IN, -PI_IN, ALU.min, ALU.max).then_inc(angle, 1)
                dve.wait_ge(angle, 8)
                dve.scalar_tensor_tensor(cosb[:, :], sinb[:, :], -1.0, sinb[:, :], ALU.mult, ALU.max).then_inc(angle, 1)
                dve.wait_ge(angle, 9)
                dve.tensor_scalar(cosb[:, :], cosb[:, :], -1.0, float(np.pi / 2), ALU.mult, ALU.add).then_inc(angle, 1)

            def rope_tables():
                dve.wait_ge(trig, 1)
                dve.tensor_copy(cosb[:, :], rot[:, S:2 * S]).then_inc(tables, 1)
                dve.tensor_scalar(sinb[:, :], rot[:, 0:S], rc[:, 1:2], None, ALU.mult).then_inc(tables, 1)

            row_sums(0)
            normalise(0, mems, mems)
            split(0)
            split(1)
            norm_lo(0, o_hi, o_lo, mgain)
            for c in range(2, LEAD):
                split(c)
            for l in range(DEPTH):
                for b in range(NB):
                    c = l * NC + 2 * b
                    s = b - FIRST_SLOT
                    if b == AT["OUT0"]:
                        mix_products(l, 7)
                    if 1 <= s <= NU:
                        weigh(l, s - 1)
                    split(c + LEAD)
                    if b == AT["MK0"] and l:
                        row_sums(1 + l)
                    if l == 0 and b == AT["KC"]:
                        rope_tables()
                    if b == AT["MK1"]:
                        normalise(1 + l, xs, xn)
                    if b == AT["MV1"]:
                        norm_lo(1 + l, h_hi, h_lo, pars[:, PAR["gain"]])
                    if 1 <= b - AT["BR0"] < 8:
                        mix_products(l, b - AT["BR0"] - 1)
                    if 2 <= b - AT["OUT0"]:
                        add_out(l, b - AT["OUT0"] - 1)
                    if b == AT["OUT1"]:
                        add_out(l, 0)
                    split(c + LEAD + 1)
                    if 0 <= s < NU:
                        maxima(l, s)
                    if b > 0 and KIND[b - 1] in ROPED:
                        shuffle(l, b - 1)
                    if b > 0 and KIND[b - 1] in GATED:
                        gate(l, b - 1)
                    if s - 2 in PV_OF:
                        out_product(l, s - 2)
                    if l == 0 and b == AT["MK0"]:
                        row_sums(1)
                    if l == 0 and b == AT["MK1"]:
                        reduce_angles()
                    if b == AT["KC"]:
                        dve.wait_ge(wg_split_hi, l + 1)
                        dve.tensor_tensor(wg_lo[:, :], pars[:, PAR["wg"]], wg_hi[:, :].bitcast(F32),
                                          ALU.subtract).then_inc(wg_split_lo, 1)
                    if b == AT["AV1"]:
                        dve.wait_ge(g_tanh, l + 1)
                        dve.tensor_scalar(gt, gt, 0.5, 0.5, ALU.mult, ALU.add).then_inc(g_half, 1)
                    if b == AT["AU0"]:
                        layernorm(l)
                    if b == AT["AU1"]:
                        layernorm_scale(l)
                    if b in (AT["WK1"], AT["WV0"]):
                        t = 0 if b == AT["WK1"] else 1
                        dve.wait_ge(mixed_a, 2 * l + t + 1)
                        dve.wait_ge(ua_ready, 2 * l + 2)
                        after(dve, oa_prod, 2 * l + t)
                        dve.tensor_tensor(ot[:, :], (mi, pv)[t][:, :], lnb[:, 2, :], ALU.add).then_inc(oa_sum, 1)
                    if b in CMP_TANH:
                        i = CMP_TANH[b]
                        dve.wait_ge(cmp_tanh, 2 * l + i + 1)
                        after(dve, cmp_mm, 2 * l + i)
                        dve.scalar_tensor_tensor(hs[:, :], hst[:, :], 1.0, tr[:, 0:32], ALU.add, ALU.mult)\
                           .then_inc(cmp_act, 1)
                if l < DEPTH - 1:
                    add_out(l, 3)
            dve.wait_ge(pars_in, 32 * DEPTH + 16)
            a = 3 * 256
            for t in range(2):
                dve.wait_ge(last_done, t + 1)
                dve.tensor_tensor(xs[:, t, a:], pj[(AT["OUT3"] + t) % 2][:, 0:256], xs[:, t, a:], ALU.add)\
                   .then_inc(last_added, 1)
                dve.wait_ge(last_added, t + 1)
                dve.tensor_tensor(xn[:, t, a:], xs[:, t, a:], lnb[:, 0:2, :].rearrange("p a n -> p (a n)")[:, a:],
                                  ALU.mult).then_inc(gained, 1)
                dve.wait_ge(squares, 4 * DEPTH + 3 + t + 1)
                dve.wait_ge(rstd_ready, 2 * (DEPTH + 1))
                dve.tensor_reduce(ss[:, t:t + 1], sq[:, t, :], AX.X, ALU.add).then_inc(summed, 1)
            dve.wait_ge(gained, 5)
            dve.wait_ge(rstd_ready, 2 * (DEPTH + 2))
            dve.tensor_scalar(xn[:, 1, :], xn[:, 1, :], rstd[:, 1:2], None, ALU.mult).then_inc(fin[1], 1)

        @block.gpsimd
        def _(pool):
            def inverse_root(n):
                for t, e in ((0, 1), (1, 2)) if n in (0, DEPTH + 1) else ((0, 2),):
                    pool.wait_ge(summed, 2 * n + e)
                    after(pool, xn_ready, 2 * n)
                    pool.tensor_scalar(ss[:, t:e], ss[:, t:e], 1.0 / D, EPS, ALU.mult, ALU.add)\
                        .then_inc(mean_sq, e - t)
                    pool.wait_ge(mean_sq, 2 * n + e)
                    pool.tensor_tensor(rstd[:, t:e], ss[:, t:e], minus_half[:, t:e], ALU.pow)\
                        .then_inc(rstd_ready, e - t)

            def rope(l, b):
                i = l * N_ROPE + count_before(ROPED, b)
                t, r, co, si = rope_view(b)
                pool.wait_ge(shuffled, i + 1)
                pool.tensor_tensor(r, r, si, ALU.mult).then_inc(rope_step, 1)
                pool.tensor_tensor(t, t, co, ALU.mult).then_inc(rope_step, 1)
                pool.wait_ge(rope_step, 2 * i + 2)
                pool.tensor_tensor(t, t, r, ALU.add).then_inc(roped, 1)

            def make_blocks(l, i):
                if i == 0:
                    pool.wait_ge(roped, n_roped(l, "KC"))
                else:
                    pool.wait_ge(copied, n_copied(l, "VC"))
                    pool.wait_ge(blk_hi, 2 * l + 1)
                    pool.wait_ge(blk_lo, 2 * l + 1)
                src = (kc, vc)[i].rearrange("p g (n l) -> p l g n", l=CS)
                pe_ = pars[:, PAR["pe_k" if i == 0 else "pe_v"]]
                for part in range(2):
                    for g in range(GROUPS):
                        ins = pool.tensor_tensor(blk[:, CS * part:CS * part + CS, g, 0:NCMP - 1],
                                                 src[:, :, g, part:part + NCMP - 1],
                                                 pe_[:, CS * part:CS * part + CS].unsqueeze(2)
                                                 .to_broadcast([P, CS, NCMP - 1]), ALU.add)
                    ins.then_inc(blk_ready, 1)
                pool.memset(blk[:, :, :, NCMP - 1:NCMP], 0.0).then_inc(blk_ready, 1)

            def split_blocks(l, i):
                pool.wait_ge(blk_hi, 2 * l + i + 1)
                pool.tensor_tensor(o_lo[:, 4 * i:4 * i + 4, :].rearrange("p a b -> p (a b)"),
                                   blk.rearrange("p l g n -> p (l g n)"),
                                   o_hi[:, 4 * i:4 * i + 4, :].rearrange("p a b -> p (a b)").bitcast(F32),
                                   ALU.subtract).then_inc(blk_lo, 1)

            def gain_part(i):
                a = 256 * i
                pool.wait_ge(x_added, 4 * (DEPTH - 1) + i + 1)
                gain = lnb[:, 0:2, :].rearrange("p a n -> p (a n)")[:, a:a + 256].unsqueeze(1).to_broadcast([P, 2, 256])
                pool.tensor_tensor(xn[:, :, a:a + 256], xs[:, :, a:a + 256], gain, ALU.mult).then_inc(gained, 1)

            pool.memset(ident[:, :], 0.0).then_inc(const_step, 1)
            pool.memset(fold[:, :], 0.0).then_inc(const_step, 1)
            pool.memset(keep[:, :, :], 1.0).then_inc(const_step, 1)
            pool.memset(ot[:, :], 0.0).then_inc(const_step, 1)
            pool.memset(minus_half[:, :], -0.5).then_inc(const_step, 1)
            pool.memset(sq[:, :, :], 0.0).then_inc(consts, 1)
            pool.wait_ge(const_step, 5)
            pool.affine_select(out=ident[:, :], in_=ident[:, :], compare_op=ALU.not_equal, fill=1.0, base=0,
                               pattern=[[-1, P]], channel_multiplier=1).then_inc(consts, 1)
            inverse_root(0)
            for j in range(4):
                pool.affine_select(out=fold[:, :], in_=fold[:, :], compare_op=ALU.not_equal, fill=1.0,
                                   base=-32 * j, pattern=[[-1, 32]], channel_multiplier=1).then_inc(const_step, 1)
                pool.wait_ge(const_step, 6 + j)
            mv0 = ot[:, 0:2 * NCMP].rearrange("p (t n) -> p t n", t=2)
            for t in range(2):
                pool.affine_select(out=mv0[:, t, :], in_=mv0[:, t, :], compare_op=ALU.is_ge, fill=NEG,
                                   base=P * t - (CB - 1), pattern=[[-CS, NCMP]],
                                   channel_multiplier=1).then_inc(const_step, 1)
                pool.affine_select(out=keep[:, t, :], in_=keep[:, t, :], compare_op=ALU.is_ge, fill=0.0,
                                   base=P * t - (CB - 1), pattern=[[-CS, NCMP]],
                                   channel_multiplier=1).then_inc(const_step, 1)
            pool.affine_select(out=ot[:, P:2 * P], in_=ot[:, P:2 * P], compare_op=ALU.is_ge, fill=NEG, base=0,
                               pattern=[[-1, P]], channel_multiplier=1).then_inc(const_step, 1)
            pool.wait_ge(const_step, 14)
            pool.wait_ge(consts, 2)
            pool.tensor_copy(identr[:, :], ident[:, :]).then_inc(consts, 1)
            for t in range(2):
                pool.tensor_copy(neg[:, t, 0:NCMP], mv0[:, t, :]).then_inc(consts, 1)
            for br in range(2):
                a = NCMP + P * br
                pool.tensor_copy(neg[:, 0, a:a + P], ot[:, P:2 * P]).then_inc(consts, 1)
                pool.tensor_copy(neg[:, 1, a:a + P], ot[:, 2 * P:3 * P]).then_inc(consts, 1)

            for l in range(DEPTH):
                for b in range(NB):
                    s = b - FIRST_SLOT
                    if b == AT["MK0"]:
                        inverse_root(1 + l)
                        pool.wait_ge(pars_in, 32 * (l + 1))
                        w = pars[:, PAR["ws"]].rearrange("p (g t) -> p g t", g=AG)
                        pool.affine_select(out=w, in_=w, compare_op=ALU.is_ge, fill=0.0, base=0,
                                           pattern=[[0, AG], [1, P]], channel_multiplier=-1).then_inc(wsm, 1)
                    if b > 0 and KIND[b - 1] in ROPED:
                        if l == 0 and KIND[b - 1] == "KC":
                            pool.wait_ge(tables, 2)
                        rope(l, b - 1)
                    if b == AT["KS"]:
                        make_blocks(l, 0)
                    if b == AT["VS"]:
                        split_blocks(l, 0)
                    if b == AT["VW"]:
                        make_blocks(l, 1)
                    if b == AT["AU0"]:
                        split_blocks(l, 1)
                        pool.wait_ge(v_stats, 4 * l + 4)
                        after(pool, vn_scaled, 2 * l)
                        pool.tensor_scalar(lstd[:, :], mvar[:, :, 1], 1.0, EPS, ALU.mult, ALU.add)\
                            .then_inc(lstd_step, 1)
                        pool.wait_ge(lstd_step, 2 * l + 1)
                        pool.tensor_tensor(lstd[:, :], lstd[:, :], minus_half[:, :], ALU.pow).then_inc(lstd_step, 1)
                    if b == AT["AZ0"]:
                        for t in range(2):
                            pool.wait_ge(vn_scaled, 2 * l + t + 1)
                            pool.tensor_tensor(vn[:, t, :], vn[:, t, :], lnb[:, 0, :], ALU.mult)\
                                .then_inc(vn_gained, 1)
                        for t in range(2):
                            pool.wait_ge(vn_gained, 2 * l + t + 1)
                            pool.tensor_tensor(vn[:, t, :], vn[:, t, :], lnb[:, 1, :], ALU.add)\
                                .then_inc(vn_ready, 1)
                    if b in (AT["WK1"], AT["WV0"]):
                        t = 0 if b == AT["WK1"] else 1
                        pool.wait_ge(oa_sum, 2 * l + t + 1)
                        pool.tensor_tensor(oa_view(t), ot[:, :].rearrange("p (g n) -> p g n", g=AG), oa_view(t),
                                           ALU.mult).then_inc(oa_prod, 1)
                    if b in OA_HI:
                        t = OA_HI[b]
                        pool.wait_ge(oa_hi, 2 * l + t + 1)
                        pool.wait_ge(oa_prod, 2 * l + t + 1)
                        pool.tensor_tensor(o_lo[:, 0:4, P * t:P * t + P], oa_view(t),
                                           o_hi[:, 0:4, P * t:P * t + P].bitcast(F32), ALU.subtract).then_inc(oa_lo, 1)
                    if s - 2 in PV_OF:
                        u = s - 2
                        pool.wait_ge(ob_hi, l * NPV + PV_OF[u] + 1)
                        pool.tensor_tensor(out_place(o_lo, u), out_source(u), out_place(o_hi, u).bitcast(F32),
                                           ALU.subtract).then_inc(ob_lo, 1)
                    if 1 <= b - AT["BR0"] <= 8:
                        i = b - AT["BR0"] - 1
                        n = 8 * l + i
                        pool.wait_ge(mix_prod, n + 1)
                        pool.tensor_tensor(mix[:, 0, :], mix[:, 0, :], mix[:, 1, :], ALU.add).then_inc(mix_add, 1)
                        pool.wait_ge(mix_add, 2 * n + 1)
                        pool.tensor_tensor(mix[:, 0, :], mix[:, 0, :], mix[:, 2, :], ALU.add).then_inc(mix_add, 1)
                        pool.wait_ge(mix_hi, n + 1)
                        pool.tensor_tensor(h_lo[:, i, :], mix[:, 0, :], h_hi[:, i, :].bitcast(F32),
                                           ALU.subtract).then_inc(mix_lo, 1)
            pool.wait_ge(pars_in, 32 * DEPTH + 16)
            for i in range(3):
                gain_part(i)
            inverse_root(DEPTH + 1)


def lay_out(a):
    w_in, w_kv, w1k, w1v = a["w_in"], a["w_mem_kv"], a["cmp_w1_k"], a["cmp_w1_v"]
    branch = np.concatenate([a["w_branch_a"], a["w_branch_b"], a["w_branch_c"]], axis=1)
    kv0 = 3 * AW + 2 * D + 24
    cq0 = kv0 + 6 * GROUPS * HD
    start = {"AU": 0, "AV": AW, "AZ": 2 * AW, "Q": 3 * AW, "BZ": 3 * AW + D, "CQ": cq0, "CZ": cq0 + AW,
             "MG": cq0 + 2 * AW}
    for i, k in enumerate(("KC", "VC", "KS", "VS", "KW", "VW")):
        start[k] = kv0 + i * GROUPS * HD
    stream = np.empty((DEPTH, NC, P, CW), np.float32)
    for l in range(DEPTH):
        for step in range(NB):
            for part, (b, half) in enumerate(halves(step)):
                k = KIND[b]
                i = int(BLOCKS[b][len(k):] or 0)
                if k in ("WK", "WV"):
                    w = (w1k if k == "WK" else w1v)[l, 8 * (2 * i + half):8 * (2 * i + half) + 8]
                    chunk = w.transpose(1, 0, 2)
                elif k == "BR":
                    w = branch[l, D * half:D * half + D, P * i:P * i + P]
                    chunk = w.reshape(KT, P, P).transpose(1, 0, 2)
                else:
                    if k in ("MK", "MV"):
                        w = w_kv[l][:, (AW if k == "MV" else 0) + 256 * i:][:, :256]
                    elif k == "OUT":
                        w = a["w_out"][l][:, 256 * i:256 * i + 256]
                    else:
                        w = w_in[l][:, start[k] + 256 * i:][:, :256]
                    if k in TOKEN_MAJOR:
                        chunk = w[512 * half:512 * half + 512].reshape(4, P, 256).transpose(1, 0, 2)
                    else:
                        chunk = w[:, P * half:P * half + P].reshape(KT, P, P).transpose(1, 0, 2)
                stream[l, 2 * step + part] = chunk.reshape(P, CW)
    par = np.empty((DEPTH, P, NPAR), np.float32)
    g0 = 3 * AW + 2 * D
    for l in range(DEPTH):
        par[l, :, PAR["gain"]] = a["norm_gain"][l].reshape(KT, P).T
        par[l, :, PAR["pe_k"]] = a["cmp_pe_k"][l].T
        par[l, :, PAR["pe_v"]] = a["cmp_pe_v"][l].T
        par[l, :, PAR["wg"]] = w_in[l][:, g0:g0 + 24].reshape(KT, P, 24).transpose(1, 0, 2).reshape(P, KT * 24)
        par[l, :, PAR["w2_k"]] = a["cmp_w2_k"][l]
        par[l, :, PAR["w2_v"]] = a["cmp_w2_v"][l]
        par[l, :, PAR["ws"]] = a["w_spatial"][l].transpose(2, 0, 1).reshape(P, AG * P)
    rows = np.stack([a["ln_v_gain"], a["ln_v_bias"], a["b_spatial"].reshape(DEPTH, AW)], axis=1)
    freq = np.float32(THETA) ** (-np.arange(0, ROT, 2, dtype=np.float32) / np.float32(ROT))
    rot_consts = np.stack([np.concatenate([freq, freq]), np.repeat(np.float32([-1, 1]), HALF)], axis=1)
    return {
        "x": a["x"].reshape(S, D), "mem": a["mem"].reshape(M, D), "positions": a["positions"].reshape(1, S),
        "stream": stream.reshape(DEPTH * NC, P, CW), "par": par, "rows": np.ascontiguousarray(rows),
        "mem_gain": np.ascontiguousarray(a["mem_norm_gain"].reshape(KT, P).T),
        "final_gain": a["final_norm_gain"].reshape(1, D), "rot_consts": rot_consts.astype(np.float32),
    }


def kernel(**inputs):
    import concourse.bacc as bacc
    from concourse.bass_utils import run_bass_kernel_spmd

    nc = bacc.Bacc("TRN2", target_bir_lowering=False, num_devices=1)
    laid = lay_out({k: np.asarray(v) for k, v in inputs.items()})
    arrays = {f"in_{k}": np.ascontiguousarray(v) for k, v in laid.items()}
    args = [nc.dram_tensor(k, v.shape, mybir.dt.from_np(v.dtype), kind="ExternalInput").ap()
            for k, v in arrays.items()]
    out = nc.dram_tensor("out_0", (S, D), F32, kind="ExternalOutput").ap()
    trunk(nc, *args, out)
    r = run_bass_kernel_spmd(nc, [arrays], core_ids=[0])
    return r.results[0]["out_0"].reshape(1, S, D)
```
